# Optimizing a Trainium2 kernel written in Bass

```python
import jax, jax.numpy as jnp
from jax import lax
import numpy as np

D_MODEL = 2048
BATCH = 1
SEQ = 256
DEPTH = 2

HEAD_DIM = 128
N_MIX_HEADS = D_MODEL // HEAD_DIM
N_ATTN_HEADS = 3 * N_MIX_HEADS // 4
N_SGU_GROUPS = N_MIX_HEADS - N_ATTN_HEADS
SGU_GROUP = HEAD_DIM
ATTN_WIDTH = N_ATTN_HEADS * HEAD_DIM
SGU_WIDTH = N_SGU_GROUPS * SGU_GROUP
MIX_IN = 3 * ATTN_WIDTH + 2 * SGU_WIDTH
CHUNK = 128
DILATED_BRANCHES = ((128, 1), (512, 4), (2048, 16))
BRANCH_BLOCK = 128
ROPE_THETA = 500000.0
ROPE_DIM = HEAD_DIM // 4
CONV_WIDTH = 3
D_FF = -(-8 * D_MODEL // (3 * 256)) * 256
N_EVEN = (DEPTH + 1) // 2
N_ODD = DEPTH // 2
EPS = 1e-6

kernel_name = "hybrid_dilated_attn_sgu_shortconv_adaln"

def rmsnorm(x, g):
    xf = x.astype(jnp.float32)
    y = xf * lax.rsqrt(jnp.mean(xf * xf, axis=-1, keepdims=True) + EPS)
    return (y * g.astype(jnp.float32)).astype(x.dtype)

def rope_tables(positions):
    inv_freq = ROPE_THETA ** (-jnp.arange(0, ROPE_DIM, 2, dtype=jnp.float32) / ROPE_DIM)
    ang = positions.astype(jnp.float32)[..., None] * inv_freq
    return jnp.cos(ang)[:, :, None, :], jnp.sin(ang)[:, :, None, :]

def apply_partial_rope(t, cos, sin):
    half = ROPE_DIM // 2
    t1 = t[..., :half].astype(jnp.float32)
    t2 = t[..., half:ROPE_DIM].astype(jnp.float32)
    rot = jnp.concatenate([t1 * cos - t2 * sin, t2 * cos + t1 * sin], axis=-1).astype(t.dtype)
    return jnp.concatenate([rot, t[..., ROPE_DIM:]], axis=-1)

def _dilated_branch(q, k, v, span, dilation):
    b, s, h, d = q.shape
    n = s // dilation
    nb = -(-n // BRANCH_BLOCK)
    pad = nb * BRANCH_BLOCK - n

    def to_sub(t):
        t = t.reshape(b, n, dilation, h, d).transpose(0, 2, 1, 3, 4)
        t = jnp.pad(t, ((0, 0), (0, 0), (0, pad), (0, 0), (0, 0)))
        return t.reshape(b, dilation, nb, BRANCH_BLOCK, h, d)

    def with_prev(t):
        prev = jnp.pad(t, ((0, 0), (0, 0), (1, 0), (0, 0), (0, 0), (0, 0)))[:, :, :nb]
        return jnp.concatenate([prev, t], axis=3)

    qs = to_sub(q)
    kb = with_prev(to_sub(k))
    vb = with_prev(to_sub(v))
    scores = jnp.einsum("brnqhd,brnkhd->brnqhk", qs, kb).astype(jnp.float32) * (d ** -0.5)

    qi = jnp.arange(BRANCH_BLOCK)[:, None]
    kj = jnp.arange(2 * BRANCH_BLOCK)[None, :]
    dist = qi + BRANCH_BLOCK - kj
    band = (dist >= 0) & (dist <= span)
    not_first = jnp.arange(nb)[:, None, None] > 0
    valid = band[None] & (not_first | (kj >= BRANCH_BLOCK)[None])
    scores = jnp.where(valid[None, None, :, :, None, :], scores, -jnp.inf)

    m = jnp.max(scores, axis=-1, keepdims=True)
    p = jnp.exp(scores - m)
    l = jnp.sum(p, axis=-1)
    o = jnp.einsum("brnqhk,brnkhd->brnqhd", p, vb.astype(jnp.float32)) / l[..., None]
    lse = m[..., 0] + jnp.log(l)

    def from_sub(t):
        t = t.reshape(b, dilation, nb * BRANCH_BLOCK, *t.shape[4:])[:, :, :n]
        t = jnp.moveaxis(t, 1, 2)
        return t.reshape(b, s, *t.shape[3:])

    return from_sub(o), from_sub(lse)

def dilated_attention(q, k, v):
    outs, lses = zip(*[_dilated_branch(q, k, v, w // dil, dil) for w, dil in DILATED_BRANCHES])
    alpha = jax.nn.softmax(jnp.stack(lses, axis=-1), axis=-1)
    o = sum(alpha[..., i, None] * outs[i] for i in range(len(outs)))
    return o.astype(q.dtype)

def spatial_gating(u, v, w_s, b_s):
    b, s, _ = u.shape
    shp = (b, s // CHUNK, CHUNK, N_SGU_GROUPS, SGU_GROUP)
    u = jax.nn.gelu(u).reshape(shp)
    v = jax.nn.gelu(v).reshape(shp)
    w = w_s * jnp.tril(jnp.ones((CHUNK, CHUNK), w_s.dtype))
    mixed = jnp.einsum("gts,bnsgc->bntgc", w, v) + b_s.T[:, :, None]
    return (u * mixed).reshape(b, s, SGU_WIDTH)

def attn_sgu_mixer(h, w_in, w_s, b_s, w_out, cos, sin):
    b, s, _ = h.shape
    z = h @ w_in
    q, k, v, u, vg = jnp.split(
        z, [ATTN_WIDTH, 2 * ATTN_WIDTH, 3 * ATTN_WIDTH, 3 * ATTN_WIDTH + SGU_WIDTH], axis=-1)
    hs = (b, s, N_ATTN_HEADS, HEAD_DIM)
    q = apply_partial_rope(q.reshape(hs), cos, sin)
    k = apply_partial_rope(k.reshape(hs), cos, sin)
    attn = dilated_attention(q, k, v.reshape(hs)).reshape(b, s, ATTN_WIDTH)
    sgu = spatial_gating(u, vg, w_s, b_s)
    return jnp.concatenate([attn, sgu], axis=-1) @ w_out

def short_conv_mixer(h, w_in, conv_w, w_out):
    gb, gc, hx = jnp.split(h @ w_in, 3, axis=-1)
    y = gc * hx
    s = y.shape[1]
    y_pad = jnp.pad(y, ((0, 0), (CONV_WIDTH - 1, 0), (0, 0)))
    conv = sum(conv_w[j] * y_pad[:, j:j + s] for j in range(CONV_WIDTH))
    return (gb * conv) @ w_out

def swiglu(h, w_gate, w_up, w_down):
    return (jax.nn.silu(h @ w_gate) * (h @ w_up)) @ w_down

def setup_inputs(seed: int = 0) -> dict:
    key = jax.random.key(seed)
    ks = jax.random.split(key, 20)
    nrm = jax.random.normal
    f32 = jnp.float32
    d = D_MODEL
    x = nrm(ks[0], (BATCH, SEQ, d), f32)
    c = nrm(ks[1], (BATCH, d), f32)
    positions = (jnp.arange(SEQ, dtype=jnp.int32)[None, :]
                 + jax.random.randint(ks[2], (BATCH, 1), 0, 4096, dtype=jnp.int32))
    ada_w = nrm(ks[3], (DEPTH, d, 6 * d), f32) * (0.5 * d ** -0.5)
    ada_b = nrm(ks[4], (DEPTH, 6 * d), f32) * 0.02
    norm_mix = 1.0 + 0.02 * nrm(ks[5], (DEPTH, d), f32)
    norm_ffn = 1.0 + 0.02 * nrm(ks[6], (DEPTH, d), f32)
    ab_w_in = nrm(ks[7], (N_EVEN, d, MIX_IN), f32) * d ** -0.5
    sgu_w = nrm(ks[8], (N_EVEN, N_SGU_GROUPS, CHUNK, CHUNK), f32) * CHUNK ** -0.5
    sgu_b = 1.0 + 0.1 * nrm(ks[9], (N_EVEN, N_SGU_GROUPS, CHUNK), f32)
    ab_w_out = nrm(ks[10], (N_EVEN, ATTN_WIDTH + SGU_WIDTH, d), f32) * (ATTN_WIDTH + SGU_WIDTH) ** -0.5
    conv_w_in = nrm(ks[11], (N_ODD, d, 3 * d), f32) * d ** -0.5
    conv_w = nrm(ks[12], (N_ODD, CONV_WIDTH, d), f32) * CONV_WIDTH ** -0.5
    conv_w_out = nrm(ks[13], (N_ODD, d, d), f32) * d ** -0.5
    ffn_w_gate = nrm(ks[14], (DEPTH, d, D_FF), f32) * d ** -0.5
    ffn_w_up = nrm(ks[15], (DEPTH, d, D_FF), f32) * d ** -0.5
    ffn_w_down = nrm(ks[16], (DEPTH, D_FF, d), f32) * D_FF ** -0.5
    final_norm = 1.0 + 0.02 * nrm(ks[17], (d,), f32)
    return {"x": x, "c": c, "positions": positions, "ada_w": ada_w, "ada_b": ada_b,
            "norm_mix": norm_mix, "norm_ffn": norm_ffn, "ab_w_in": ab_w_in,
            "sgu_w": sgu_w, "sgu_b": sgu_b, "ab_w_out": ab_w_out,
            "conv_w_in": conv_w_in, "conv_w": conv_w, "conv_w_out": conv_w_out,
            "ffn_w_gate": ffn_w_gate, "ffn_w_up": ffn_w_up, "ffn_w_down": ffn_w_down,
            "final_norm": final_norm}

def reference(x, c, positions, ada_w, ada_b, norm_mix, norm_ffn, ab_w_in, sgu_w, sgu_b,
              ab_w_out, conv_w_in, conv_w, conv_w_out, ffn_w_gate, ffn_w_up, ffn_w_down,
              final_norm):
    cos, sin = rope_tables(positions)
    c_act = jax.nn.silu(c)
    for layer in range(DEPTH):
        mod = (c_act @ ada_w[layer] + ada_b[layer])[:, None, :]
        sh_m, sc_m, g_m, sh_f, sc_f, g_f = jnp.split(mod, 6, axis=-1)
        h = rmsnorm(x, norm_mix[layer]) * (1 + sc_m) + sh_m
        i = layer // 2
        if layer % 2 == 0:
            mix = attn_sgu_mixer(h, ab_w_in[i], sgu_w[i], sgu_b[i], ab_w_out[i], cos, sin)
        else:
            mix = short_conv_mixer(h, conv_w_in[i], conv_w[i], conv_w_out[i])
        x = x + g_m * mix
        h = rmsnorm(x, norm_ffn[layer]) * (1 + sc_f) + sh_f
        x = x + g_f * swiglu(h, ffn_w_gate[layer], ffn_w_up[layer], ffn_w_down[layer])
    return rmsnorm(x, final_norm)


_drawn_inputs = setup_inputs


def setup_inputs(seed=0):
    import zlib

    import numpy as np

    out = dict(_drawn_inputs(seed))
    spreads = {}
    factors = {'norm_mix': 4.439, 'norm_ffn': 6.395, 'sgu_b': 4.6, 'final_norm': 2.832}
    for name, (base, spread) in spreads.items():
        noise = np.random.default_rng([zlib.crc32(name.encode()), seed]).standard_normal(out[name].shape)
        drawn = base * np.exp(spread * noise) if base else spread * noise
        out[name] = __import__('jax').numpy.asarray(drawn.astype(out[name].dtype))
    for name, factor in factors.items():
        out[name] = (out[name] * factor).astype(out[name].dtype)
    return out
```

```python
from contextlib import ExitStack

import numpy as np

import concourse.bass as bass
from concourse import mybir

F32 = mybir.dt.float32
F32R = mybir.dt.float32r
I32 = mybir.dt.int32
ALU = mybir.AluOpType
ACT = mybir.ActivationFunctionType
AX_X = mybir.AxisListType.X

P = 128
D = 2048
S = 256
KT = D // P
HEADS = 12
GROUPS = 4
D_FF = 5632
MIX_TILES = 5632 // P
CHUNKS = D_FF // 512
SCALE = float(P) ** -0.5
EPS = 1e-6
ROPE_DIM = 32
ROPE_THETA = 500000.0
MASKED = -1e30
BRANCHES = ((128, 1), (512, 4), (2048, 16))
HALF_PI = float(np.pi / 2)
SIN_MAX = 3.1415925
TWO_PI_A = 6.28125
TWO_PI_B = round((2 * np.pi - TWO_PI_A) * 2**19) / 2**19
TWO_PI_C = 2 * np.pi - TWO_PI_A - TWO_PI_B
ROUND = 12582912.0

RAW = 4
PAIR = 2
BANKS = 8
COLS = 512
ADA_SLOTS = 4
PIECES = KT // 2
ADA_GROUPS = 6 * D // COLS
SH_M, SC_M, G_M, SH_F, SC_F, G_F = range(6)

U_IN, U_OUT, U_F0, U_CI, U_CI2, U_CO, U_F1, U_END = 0, 44, 60, 192, 224, 240, 256, 388
T_IN, T_OUT, T_F0, T_CI, T_CI2, T_CO, T_F1, T_END = 0, 44, 60, 324, 356, 372, 388, 652
V_IN, V_OUT, V_F0, V_CI, V_CO, V_F1 = 0, 33, 45, 111, 147, 159
J_IN, J_ATT, J_OUT, J_F0, J_CI, J_CI2, J_CO, J_END = 9, 20, 23, 27, 38, 42, 44, 48
X_OUT, X_F0, X_CO, X_F1, X_END = 0, 16, 192, 208, 384
H_N0, H_MIX, H_N1, H_N2, H_CONV, H_N3 = (KT * n for n in range(6))
NORM_BANK = 7
ROPE_ORDER = [b + 6 * s for b in range(6) for s in range(2)]


def mod_column(layer, which, n):
    return 6 * KT * layer + KT * which + n


def decoder_kernel(nc, xT, c_col, pos, ada_w, ada_b, g_mix, g_ffn, w_in, sgu_w, sgu_b, w_out,
                   conv_in, conv_w, conv_out, ff_gate, ff_up, ff_down, g_fin, rope_const, ident_in,
                   mask_in, outT):
    with ExitStack() as ctx:
        def sb(name, shape, dt=F32):
            return ctx.enter_context(nc.sbuf_tensor(name, shape, dt))

        def sems(names):
            return [ctx.enter_context(nc.semaphore(n)) for n in names.split()]

        x = sb("x", [P, KT, S])
        h = sb("h", [P, KT, 2 * S], F32R)
        z = sb("z", [P, 48, S])
        raw = sb("raw", [P, RAW, 4, COLS])
        whi = [sb(f"whi{s}", [P, 4, COLS], F32R) for s in range(PAIR)]
        wlo = [sb(f"wlo{s}", [P, 4, COLS], F32R) for s in range(PAIR)]
        ada = sb("ada", [P, ADA_SLOTS, 2, COLS])
        acc = sb("acc", [P, 3, COLS])
        scratch = sb("scratch", [P, 2048])
        half = scratch[:, 0:1024].rearrange("p (s t) -> p s t", s=4)
        xt = scratch[:, 1024:2048].rearrange("p (s t) -> p s t", s=4)
        act = sb("act", [P, 4, 2 * S], F32R)
        gu = sb("gu", [P, 2, 2, S])
        rstd = sb("rstd", [P, S])
        mod = sb("mod", [P, 12 * KT])
        adab = sb("adab", [P, 12 * KT])
        gain = sb("gain", [P, 5, KT])
        gsc = sb("gsc", [P, KT])
        cact = sb("cact", [P, KT])
        cwt = sb("cwt", [P, 3, KT])
        eps = sb("eps", [P, 2])
        ones = sb("ones", [P, P])
        ident = sb("ident", [P, P])
        mask = sb("mask", [P, 3 * P])
        rc = sb("rc", [ROPE_DIM, 2 + ROPE_DIM])
        tables = sb("tables", [ROPE_DIM + 1, 2 * S])
        cosT, sinT = tables[0:ROPE_DIM, 0:S], tables[0:ROPE_DIM, S:2 * S]
        sgub = tables[ROPE_DIM:ROPE_DIM + 1, :]
        mx, nmx, den, rden = (rstd[:, 2 * HEADS * n:2 * HEADS * (n + 1)].rearrange("p (i q) -> p i q", q=2)
                              for n in range(4))
        prob = scratch[:, 0:768].rearrange("p (s t) -> p s t", s=2)
        probT = scratch[:, 768:1536].rearrange("p (s t) -> p s t", s=2)
        vtok = scratch[:, 1536:2048].rearrange("p (s t) -> p s t", s=2)
        gflat = gu[:, :, :, :].rearrange("p a b t -> p (a b t)")
        rot = gflat[0:ROPE_DIM, :].rearrange("p (s t) -> p s t", s=2)
        vgt = gflat.rearrange("p (g t) -> p g t", g=GROUPS)
        gu4 = gflat.rearrange("p (g t) -> p g t", g=4)
        wst = z[:, 44:46, :].rearrange("p a t -> p (a t)")
        wsr = z[:, 46:48, :].rearrange("p a t -> p (a t)")
        posi = z[0:ROPE_DIM, 40, :].bitcast(I32)
        ang, turns, angc = (z[0:ROPE_DIM, 41 + n, :] for n in range(3))

        ps = ctx.enter_context(nc.psum_tensor("ps", [P, BANKS, COLS], F32))

        raw_loaded = sems(" ".join(f"raw_loaded{s}" for s in range(RAW)))
        ada_loaded = sems(" ".join(f"ada_loaded{s}" for s in range(ADA_SLOTS)))
        x_loaded, const_loaded, pos_loaded, c_loaded, sgu_loaded, out_stored = sems(
            "x_loaded const_loaded pos_loaded c_loaded sgu_loaded out_stored")
        hi_ready, lo_ready, unit_used = sems("hi_ready lo_ready unit_used")
        tile_done, tile_free, half_ready, x_done = sems("tile_done tile_free half_ready x_done")
        ada_step, acc_ready, red_done, mod_done = sems("ada_step acc_ready red_done mod_done")
        silu_ready, up_step, act_ready = sems("silu_ready up_step act_ready")
        h_step, h_hi, h_ready, gsc_ready = sems("h_step h_hi h_ready gsc_ready")
        sq_ready, ms_ready, std_ready, rstd_ready = sems("sq_ready ms_ready std_ready rstd_ready")
        pool_const, cact_ready, tril_ready = sems("pool_const cact_ready tril_ready")
        ang_step, sin_ready, rope_ready = sems("ang_step sin_ready rope_ready")
        rot_done, rot_used, cos_done, rope_done = sems("rot_done rot_used cos_done rope_done")
        sc_done, sc_used, mx_done, nmx_ready, e_done, rden_done, p_ready = sems(
            "sc_done sc_used mx_done nmx_ready e_done rden_done p_ready")
        pt_done, pt_ready, v_done, v_ready, o_done = sems("pt_done pt_ready v_done v_ready o_done")
        gelu_ready, sgt_done, sgt_ready, mixed_done, gated = sems("gelu_ready sgt_done sgt_ready mixed_done gated")
        conv_prod, conv_step, conv_sum, conv_out_ready = sems("conv_prod conv_step conv_sum conv_out_ready")
        out_ready, = sems("out_ready")
        N_CONST = 9

        def rows(w):
            return w.rearrange("(t p) n -> p t n", p=P)

        def layer_rows(w):
            return w.rearrange("l (t p) n -> l p t n", p=P)

        ada_v, gate_v, up_v, down_v = (layer_rows(w) for w in (ada_w, ff_gate, ff_up, ff_down))
        w_in_v, w_out_v, conv_in_v, conv_out_v = (rows(w) for w in (w_in, w_out, conv_in, conv_out))

        block = ctx.enter_context(nc.Block())

        @block.sync
        def _(sp):
            def load_unit(u, r, pieces, first=False):
                if not first:
                    sp.wait_ge(lo_ready, u - RAW + 1)
                for dst, src in pieces:
                    sp.dma_start(dst, src).then_inc(raw_loaded[r], 32 // len(pieces))

            def load_ada(j, layer, col, q0, q1, first=False):
                for q in range(q0, q1):
                    if not (first and q < ADA_SLOTS):
                        sp.wait_ge(ada_step, 2 * (PIECES * j + q - ADA_SLOTS + 1))
                    sp.dma_start(ada[:, q % ADA_SLOTS], ada_v[layer, :, 2 * q:2 * q + 2, bass.ds(col, COLS)])\
                        .then_inc(ada_loaded[q % ADA_SLOTS], 16)

            def load_group(u, w, col, j=None, layer=0, first=False, q0=0, n=2):
                for k in range(4):
                    if j is not None:
                        load_ada(j, layer, (j - ADA_GROUPS * layer) * COLS, q0 + n * k, q0 + n * k + n)
                    load_unit(u + k, k, [(raw[:, k], w[:, 4 * k:4 * k + 4, bass.ds(col, COLS)])], first)

            def load_chunk(u, layer, c, j=None):
                for n in range(12):
                    g, k = n // 4, n % 4
                    if j is not None and 2 <= n < 10:
                        load_ada(j, 1, (j - ADA_GROUPS) * COLS, n - 2, n - 1)
                    if n < 8:
                        load_unit(u + n, k, [(raw[:, k, :, 256 * a:256 * a + 256],
                                              w[layer, :, 4 * k:4 * k + 4, bass.ds(512 * c + 256 * g, 256)])
                                             for a, w in enumerate((gate_v, up_v))])
                    else:
                        load_unit(u + n, k, [(raw[:, k], down_v[layer, :, bass.ds(4 * c, 4), COLS * k:COLS * k + COLS])])

            sp.dma_start(cact[:, :], c_col).then_inc(c_loaded, 16)
            load_ada(0, 0, 0, 0, ADA_SLOTS, first=True)
            sp.dma_start(x[:, :, :], xT.rearrange("(t p) s -> p t s", p=P)).then_inc(x_loaded, 16)
            load_ada(0, 0, 0, ADA_SLOTS, PIECES, first=True)
            with sp.Fori(1, J_IN) as j:
                load_ada(j, 0, j * COLS, 0, PIECES)
            load_group(U_IN, w_in_v, 0, first=True)
            with sp.Fori(0, 5) as i:
                for g in range(2):
                    load_group(U_IN + 4 + 8 * i + 4 * g, w_in_v, (2 * i + 1 + g) * COLS, J_IN + 2 * i + g)
            load_group(U_OUT, w_out_v, 0, J_ATT - 1)
            with sp.Fori(J_ATT, J_OUT) as j:
                load_ada(j, 0, j * COLS, 0, PIECES)
            load_group(U_OUT + 4, w_out_v, COLS, J_OUT)
            for g in range(2, 4):
                load_group(U_OUT + 4 * g, w_out_v, g * COLS, J_OUT + g - 1, 1)
            load_ada(J_F0 - 1, 1, (J_F0 - 1 - ADA_GROUPS) * COLS, 0, PIECES)
            with sp.Fori(0, CHUNKS) as c:
                load_chunk(U_F0 + 12 * c, 0, c, J_F0 + c)
            load_group(U_CI, conv_in_v, 0)
            with sp.Fori(0, 5) as i:
                for g in range(2):
                    load_group(U_CI + 4 + 8 * i + 4 * g, conv_in_v, (2 * i + g + 1) * COLS, J_CI + i, 1, q0=4 * g, n=1)
            load_group(U_CI + 44, conv_in_v, 11 * COLS, J_CO - 1, 1, q0=0, n=1)
            load_group(U_CO, conv_out_v, 0, J_CO - 1, 1, q0=4, n=1)
            for g in range(1, 4):
                load_group(U_CO + 4 * g, conv_out_v, g * COLS, J_CO + g - 1, 1)
            load_ada(J_END - 1, 1, (J_END - 1 - ADA_GROUPS) * COLS, 0, PIECES)
            with sp.Fori(0, CHUNKS) as c:
                load_chunk(U_F1 + 12 * c, 1, c)
            for n in range(4):
                sp.wait_ge(out_ready, 4 * n + 4)
                sp.dma_start(outT.rearrange("(t p) s -> p t s", p=P)[:, 4 * n:4 * n + 4, :],
                             z[:, 32 + 4 * n:36 + 4 * n, :]).then_inc(out_stored, 16)
            sp.wait_ge(out_stored, 64)

        @block.gpsimd
        def _(pool):
            def add_residual(T, n):
                pool.wait_ge(tile_free, BANKS + T + 1)
                nc.gpsimd.tensor_tensor(x[:, n, :], x[:, n, :], xt[:, n % 4, :], ALU.add).then_inc(x_done, 1)

            nc.gpsimd.memset(ones[:, :], 1.0).then_inc(pool_const, 1)
            nc.gpsimd.memset(eps[:, 0:1], EPS).then_inc(pool_const, 1)
            nc.gpsimd.memset(eps[:, 1:2], 0.0).then_inc(x_done, 4)
            pool.wait_ge(sgu_loaded, 16)
            wsr3 = wsr.rearrange("p (g s) -> p g s", g=GROUPS)
            nc.gpsimd.affine_select(out=wsr3, in_=wsr3, compare_op=ALU.is_ge, fill=0.0, base=0,
                                    pattern=[[0, GROUPS], [-1, P]], channel_multiplier=1).then_inc(tril_ready, 1)
            pool.wait_ge(rope_ready, 1)
            pool.wait_ge(sin_ready, 2)
            for n, b in enumerate(ROPE_ORDER):
                pool.wait_ge(rot_done, n + 1)
                zz = z[0:ROPE_DIM, 2 * b:2 * b + 2, :]
                nc.gpsimd.tensor_tensor(zz, zz, cosT.unsqueeze(1).to_broadcast([ROPE_DIM, 2, S]), ALU.mult)\
                    .then_inc(cos_done, 1)
            with pool.Fori(0, 2) as i:
                for n in range(8):
                    pool.wait_ge(tile_free, BANKS + T_OUT + 8 * i + n + 1)
                    xn = x[:, bass.ds(8 * i + n, 1), :]
                    nc.gpsimd.tensor_tensor(xn, xn, xt[:, n % 4:n % 4 + 1, :], ALU.add).then_inc(x_done, 1)
            with pool.Fori(0, CHUNKS) as c:
                for n in range(KT):
                    add_residual(T_F0 + 24 * c + 8 + n, n)
            with pool.Fori(0, 4) as i:
                for n in range(4):
                    pool.wait_ge(tile_free, BANKS + T_CI2 + 4 * i + n + 1)
                    hx = z[:, bass.ds(32 + 4 * i + n, 1), :]
                    nc.gpsimd.tensor_tensor(hx, z[:, bass.ds(16 + 4 * i + n, 1), :], hx, ALU.mult).then_inc(conv_prod, 1)
                for n in range(4):
                    pool.wait_ge(conv_sum, 4 * i + n + 1)
                    gb = z[:, bass.ds(4 * i + n, 1), :]
                    nc.gpsimd.tensor_tensor(gb, gb, gu4[:, n:n + 1, :], ALU.mult).then_inc(conv_out_ready, 1)
            for n in range(KT):
                add_residual(T_CO + n, n)
            with pool.Fori(0, CHUNKS) as c:
                for n in range(KT):
                    add_residual(T_F1 + 24 * c + 8 + n, n)

        @block.scalar
        def _(sa):
            def round_unit(used, fills, r, s):
                if used is not None:
                    sa.wait_ge(unit_used, used)
                sa.wait_ge(raw_loaded[r], 32 * fills)
                nc.scalar.activation(whi[s][:, :, :], raw[:, r], ACT.Copy).then_inc(hi_ready, 1)

            def cross_out(T, n, scale=None):
                sa.wait_ge(tile_done, T + 1)
                sa.wait_ge(tile_free, T + 5)
                nc.scalar.activation(half[:, n % 4, :], ps[:, n % BANKS, S:2 * S],
                                     ACT.Copy if scale is None else ACT.Identity,
                                     scale=1.0 if scale is None else scale).then_inc(half_ready, 1)

            def group(used, fills, T, b, scale=None):
                for k in range(4):
                    if k == 3:
                        for n in range(4):
                            cross_out(T + n, b + n, None if scale is None else scale(n))
                    round_unit(used + k + 1 if k < 3 else None, fills + (k + 2) // RAW + 1, (k + 2) % RAW, k % PAIR)

            def chunk(used, fills, T, layer, F, last=False):
                for n in range(12):
                    if n in (3, 7):
                        g = n // 4
                        t, b = T + 4 * g, 4 + 4 * g
                        for m in range(3):
                            cross_out(t + m, b + m)
                        sa.wait_ge(tile_free, BANKS + t + 1)
                        nc.scalar.activation(gu[:, 0, 0, :], gu[:, 0, 0, :], ACT.Silu).then_inc(silu_ready, 1)
                        cross_out(t + 3, b + 3)
                        sa.wait_ge(tile_free, BANKS + t + 3)
                        nc.scalar.activation(gu[:, 1, 0, :], gu[:, 1, 0, :], ACT.Silu).then_inc(silu_ready, 1)
                    if n >= 8:
                        g = n - 8
                        if g == 0:
                            sa.wait_ge(mod_done, ADA_GROUPS * layer + 4 * G_F + 4)
                        for m in range(4):
                            col = mod_column(layer, G_F, 4 * g + m)
                            cross_out(T + 8 + 4 * g + m, 4 + 4 * g + m, mod[:, col:col + 1])
                    if not (last and n >= 10):
                        round_unit(used + 3 * (n // 4) + n % 4 + 1 if n < 8 and n % 4 < 3 else None,
                                   fills + (n + 2) // RAW + 1, (n + 2) % RAW, n % PAIR)

            def norm(k, X):
                if k:
                    sa.wait_ge(x_done, X)
                else:
                    sa.wait_ge(x_loaded, 16)
                for n in range(0, 12, 4):
                    nc.scalar.activation(z[:, n:n + 4, :], x[:, n:n + 4, :], ACT.Square).then_inc(sq_ready, 1)
                for n in range(12, KT):
                    if k:
                        sa.wait_ge(x_done, X + n - 11)
                    nc.scalar.activation(z[:, n, :], x[:, n, :], ACT.Square).then_inc(sq_ready, 1)
                sa.wait_ge(ms_ready, k + 1)
                nc.scalar.activation(rstd[:, :], ps[:, NORM_BANK, 0:S], ACT.Sqrt, bias=eps[:, 0:1], scale=1.0 / D)\
                    .then_inc(std_ready, 1)

            def norm_hi(k, base, layer, which):
                sa.wait_ge(mod_done, ADA_GROUPS * layer + 4 * which + 4)
                for n in range(KT):
                    sa.wait_ge(h_step, KT * k + n + 1)
                    col = mod_column(layer, which, n)
                    nc.scalar.activation(h[:, n, 0:S], xt[:, n % 4, :], ACT.Identity, bias=mod[:, col:col + 1])\
                        .then_inc(h_hi, 1)

            sa.wait_ge(c_loaded, 16)
            nc.scalar.activation(cact[:, :], cact[:, :], ACT.Silu).then_inc(cact_ready, 1)
            for dst, src in ((rc[:, :], rope_const), (adab[:, :], ada_b), (gain[:, 0:2, :], g_mix),
                             (gain[:, 2:4, :], g_ffn), (gain[:, 4, :], g_fin), (cwt[:, :, :], conv_w),
                             (ident[:, :], ident_in), (mask[:, :], mask_in), (sgub, sgu_b)):
                sa.dma_start(dst, src).then_inc(const_loaded, 16)
            sa.dma_start(posi, pos).then_inc(pos_loaded, 16)
            sa.dma_start(wsr.rearrange("p (g s) -> p g s", g=GROUPS), sgu_w).then_inc(sgu_loaded, 16)
            sa.wait_ge(ang_step, 11)
            nc.scalar.activation(sinT, ang, ACT.Sin).then_inc(sin_ready, 1)
            nc.scalar.activation(cosT, angc, ACT.Sin).then_inc(sin_ready, 1)
            sa.wait_ge(pool_const, 2)
            norm(0, None)
            round_unit(None, 1, 0, 0)
            round_unit(None, 1, 1, 1)
            norm_hi(0, H_N0, 0, SH_M)
            group(0, 0, T_IN, 0)
            with sa.Fori(0, 5) as i:
                for g in range(2):
                    group(V_IN + 3 + 3 * g + 6 * i, 1 + g + 2 * i, T_IN + 4 + 4 * g + 8 * i, 4 + 4 * g)

            sa.wait_ge(tile_free, BANKS + T_OUT)
            nc.scalar.activation(z[:, 36:44, :], z[:, 36:44, :], ACT.Gelu_apprx_tanh).then_inc(gelu_ready, 1)
            for i in range(HEADS + 2):
                if 1 <= i <= HEADS:
                    a = i - 1
                    sa.wait_ge(pt_done, a + 1)
                    if a >= 2:
                        sa.wait_ge(o_done, a - 1)
                    nc.scalar.activation(probT[:, a % 2, :], ps[:, 2 + a % 2, 0:3 * P], ACT.Copy).then_inc(pt_ready, 1)
                if i < HEADS:
                    sa.wait_ge(nmx_ready, i + 1)
                    for q, (a, b) in enumerate(((0, P), (P, 3 * P))):
                        nc.scalar.activation(prob[:, i % 2, a:b], prob[:, i % 2, a:b], ACT.Exp, bias=nmx[:, i, q:q + 1],
                                             accum_out=den[:, i, q:q + 1]).then_inc(e_done, 1)
                    sa.wait_ge(v_done, i + 1)
                    if i >= 2:
                        sa.wait_ge(o_done, i - 1)
                    nc.scalar.activation(vtok[:, i % 2, :], ps[:, 6 + i % 2, 0:S], ACT.Copy).then_inc(v_ready, 1)
                if i >= 2:
                    a = i - 2
                    sa.wait_ge(o_done, a + 1)
                    nc.scalar.activation(h[:, a, 0:S], ps[:, 4 + a % 2, 0:S], ACT.Copy).then_inc(h_hi, 1)
            for n in range(3):
                sa.wait_ge(sgt_done, n + 1)
                nc.scalar.activation(wst if n == 2 else gflat[:, COLS * n:COLS * n + COLS], ps[:, n, :], ACT.Copy)\
                    .then_inc(sgt_ready, 1)
            sa.wait_ge(gated, GROUPS)
            nc.scalar.activation(h[:, HEADS:KT, 0:S], z[:, 36:40, :], ACT.Copy).then_inc(h_hi, GROUPS)

            sa.wait_ge(mod_done, 4 * G_M + 4)
            with sa.Fori(0, 2) as i:
                for g in range(2):
                    group(V_OUT + 3 * g + 6 * i, U_OUT // RAW + g + 2 * i, T_OUT + 4 * g + 8 * i, 4 + 4 * g,
                          lambda n: mod[:, bass.ds(mod_column(0, G_M, 4 * g + n) + 8 * i, 1)])
            norm(1, X_F0)
            norm_hi(1, H_N1, 0, SH_F)
            with sa.Fori(0, CHUNKS) as c:
                chunk(V_F0 + 6 * c, U_F0 // RAW + 3 * c, T_F0 + 24 * c, 0, 4 * c)
            norm(2, X_CO)
            norm_hi(2, H_N2, 1, SH_M)
            with sa.Fori(0, 6) as i:
                for g in range(2):
                    group(V_CI + 3 * g + 6 * i, U_CI // RAW + g + 2 * i, T_CI + 4 * g + 8 * i, 4 + 4 * g)
            for n in range(4):
                sa.wait_ge(conv_out_ready, 4 * n + 4)
                nc.scalar.activation(h[:, 4 * n:4 * n + 4, 0:S], z[:, 4 * n:4 * n + 4, :], ACT.Copy).then_inc(h_hi, 4)
            sa.wait_ge(mod_done, ADA_GROUPS + 4 * G_M + 4)
            for g in range(4):
                group(V_CO + 3 * g, U_CO // RAW + g, T_CO + 4 * g, 4 + 4 * g,
                      lambda n: mod[:, mod_column(1, G_M, 4 * g + n):mod_column(1, G_M, 4 * g + n) + 1])
            norm(3, X_F1)
            norm_hi(3, H_N3, 1, SH_F)
            with sa.Fori(0, CHUNKS - 1) as c:
                chunk(V_F1 + 6 * c, U_F1 // RAW + 3 * c, T_F1 + 24 * c, 1, 4 * c)
            chunk(V_F1 + 6 * (CHUNKS - 1), (U_END - 12) // RAW, T_END - 24, 1, 4 * (CHUNKS - 1), last=True)
            norm(4, X_END)

        @block.vector
        def _(ve):
            def rest_unit(u, r, s):
                ve.wait_ge(hi_ready, u + 1)
                nc.vector.tensor_tensor(wlo[s][:, :, :], raw[:, r], whi[s][:, :, :].bitcast(F32), ALU.subtract)\
                    .then_inc(lo_ready, 1)

            def sum_ada(j, q0, q1, first=False):
                for q in range(q0, q1):
                    ve.wait_ge(ada_loaded[q % ADA_SLOTS], 16 * (2 * j + q // ADA_SLOTS + 1))
                    if q == 0 and not first:
                        ve.wait_ge(acc_ready, j)
                    for e in range(2):
                        src, c = ada[:, q % ADA_SLOTS, e, :], cact[:, 2 * q + e:2 * q + e + 1]
                        if q == 0:
                            nc.vector.tensor_scalar(acc[:, e, :], src, c, None, ALU.mult).then_inc(ada_step, 1)
                        else:
                            ve.wait_ge(ada_step, 2 * PIECES * j + 2 * q + e - 1)
                            nc.vector.scalar_tensor_tensor(out=acc[:, e, :], in0=src, scalar=c, in1=acc[:, e, :],
                                                           op0=ALU.mult, op1=ALU.add).then_inc(ada_step, 1)
                if q1 == PIECES:
                    ve.wait_ge(ada_step, 2 * PIECES * (j + 1))
                    nc.vector.tensor_tensor(acc[:, 2, :], acc[:, 0, :], acc[:, 1, :], ALU.add).then_inc(acc_ready, 1)

            def keep_mod(j, b, col=0):
                ve.wait_ge(red_done, j + 1)
                nc.vector.tensor_tensor(mod[:, bass.ds(4 * j, 4)], ps[:, b % BANKS, col:col + 4], adab[:, bass.ds(4 * j, 4)],
                                        ALU.add).then_inc(mod_done, 1)

            def to_z(T, b, at):
                ve.wait_ge(half_ready, T + 1)
                nc.vector.tensor_tensor(z[:, bass.ds(at, 1), :], ps[:, b % BANKS:b % BANKS + 1, 0:S],
                                        half[:, b % 4:b % 4 + 1, :], ALU.add).then_inc(tile_free, 1)

            def to_x(T, b, X, scale):
                ve.wait_ge(half_ready, T + 1)
                ve.wait_ge(x_done, X + 1)
                nc.vector.scalar_tensor_tensor(out=xt[:, b % 4, :], in0=ps[:, b % BANKS, 0:S], scalar=scale,
                                               in1=half[:, b % 4, :], op0=ALU.mult, op1=ALU.add).then_inc(tile_free, 1)

            def group(u, T, b, out, j, kept=None, q0=0, p=2):
                for k in range(4):
                    if k == 3 and kept is not None:
                        keep_mod(kept, b + 7)
                    sum_ada(j, q0 + p * k, q0 + p * k + p)
                    if k == 3:
                        for n in range(4):
                            out(T + n, b + n, n)
                    rest_unit(u + k + 2, (k + 2) % RAW, k % PAIR)

            def hidden(T, b, F, g):
                if g:
                    ve.wait_ge(act_ready, F)
                def whole(m):
                    ve.wait_ge(half_ready, T + m + 1)
                    nc.vector.tensor_tensor(gu[:, m // 2, m % 2, :], ps[:, (b + m) % BANKS, 0:S], half[:, m, :],
                                            ALU.add).then_inc(tile_free, 1)

                def gated(f):
                    ve.wait_ge(tile_free, BANKS + T + 2 * f + 2)
                    ve.wait_ge(silu_ready, F + f + 1)
                    nc.vector.tensor_tensor(gu[:, f, 1, :], gu[:, f, 1, :], gu[:, f, 0, :], ALU.mult).then_inc(up_step, 1)

                def split(f):
                    ve.wait_ge(up_step, 2 * (F + f) + 1)
                    nc.vector.tensor_copy(act[:, 2 * g + f, 0:S], gu[:, f, 1, :]).then_inc(up_step, 1)
                    ve.wait_ge(up_step, 2 * (F + f) + 2)
                    nc.vector.tensor_tensor(act[:, 2 * g + f, S:2 * S], gu[:, f, 1, :],
                                            act[:, 2 * g + f, 0:S].bitcast(F32), ALU.subtract).then_inc(act_ready, 1)

                whole(0)
                whole(1)
                whole(2)
                gated(0)
                split(0)
                whole(3)
                gated(1)
                split(1)

            def chunk(u, T, X, layer, F, j=None, kept=None, last=False):
                for n in range(12):
                    if n == 3 and kept is not None:
                        keep_mod(kept, 4 + 7)
                    if n < 8 and n % 4 < 3 and j is not None:
                        sum_ada(j, n, n + 1)
                    if n in (3, 7):
                        hidden(T + n - 3, 4 + n - 3, F + n // 4 * 2, n // 4)
                    if n >= 8:
                        for m in range(4):
                            o = 4 * (n - 8) + m
                            col = mod_column(layer, G_F, o)
                            to_x(T + 8 + o, 4 + o, X + o, mod[:, col:col + 1])
                    if not (last and n >= 10):
                        rest_unit(u + n + 2, (n + 2) % RAW, n % PAIR)
                    if n in (3, 7) and j is not None:
                        sum_ada(j, n, n + 1)

            def norm_scale(k):
                ve.wait_ge(std_ready, k + 1)
                nc.vector.reciprocal(rstd[:, :], rstd[:, :]).then_inc(rstd_ready, 1)

            def norm(k, base, layer, sh, g):
                ve.wait_ge(mod_done, ADA_GROUPS * layer + 4 * (sh + 1) + 4)
                sc = mod_column(layer, sh + 1, 0)
                nc.vector.scalar_tensor_tensor(out=gsc[:, :], in0=mod[:, sc:sc + KT], scalar=1.0, in1=gain[:, g, :],
                                               op0=ALU.add, op1=ALU.mult).then_inc(gsc_ready, 1)
                if k:
                    norm_scale(k)
                ve.wait_ge(gsc_ready, k + 1)
                ve.wait_ge(rstd_ready, k + 1)
                for n in range(KT + 2):
                    if n < KT:
                        if n >= 4:
                            ve.wait_ge(h_ready, base + n - 3)
                        nc.vector.scalar_tensor_tensor(out=xt[:, n % 4, :], in0=x[:, n, :], scalar=gsc[:, n:n + 1],
                                                       in1=rstd[:, :], op0=ALU.mult, op1=ALU.mult).then_inc(h_step, 1)
                    if n >= 2:
                        m = n - 2
                        col = mod_column(layer, sh, m)
                        ve.wait_ge(h_hi, base + m + 1)
                        nc.vector.scalar_tensor_tensor(out=h[:, m, S:2 * S], in0=xt[:, m % 4, :],
                                                       scalar=mod[:, col:col + 1], in1=h[:, m, 0:S].bitcast(F32),
                                                       op0=ALU.add, op1=ALU.subtract).then_inc(h_ready, 1)

            nc.vector.memset(gu[:, :, :, :], 0.0).then_inc(tile_free, BANKS)
            ve.wait_ge(cact_ready, 1)
            sum_ada(0, 0, PIECES, first=True)
            ve.wait_ge(const_loaded, 16 * N_CONST)
            ve.wait_ge(pos_loaded, 16)
            steps = [0]

            def angle(ins):
                steps[0] += 1
                ins.then_inc(ang_step, 1)
                ve.wait_ge(ang_step, steps[0])

            angle(nc.vector.tensor_copy(ang, posi))
            angle(nc.vector.tensor_scalar(ang, ang, rc[:, 0:1], None, ALU.mult))
            angle(nc.vector.tensor_scalar(turns, ang, 1.0 / (2 * np.pi), ROUND, ALU.mult, ALU.add))
            angle(nc.vector.tensor_scalar(turns, turns, -ROUND, None, ALU.add))
            for part in (TWO_PI_A, TWO_PI_B, TWO_PI_C):
                angle(nc.vector.scalar_tensor_tensor(out=ang, in0=turns, scalar=-part, in1=ang,
                                                     op0=ALU.mult, op1=ALU.add))
            angle(nc.vector.tensor_scalar(angc, ang, HALF_PI, -2 * np.pi, ALU.is_gt, ALU.mult))
            angle(nc.vector.scalar_tensor_tensor(out=angc, in0=angc, scalar=HALF_PI, in1=ang, op0=ALU.add, op1=ALU.add))
            angle(nc.vector.tensor_scalar(ang, ang, SIN_MAX, -SIN_MAX, ALU.min, ALU.max))
            angle(nc.vector.tensor_scalar(angc, angc, SIN_MAX, -SIN_MAX, ALU.min, ALU.max))
            with ve.Fori(1, J_IN) as j:
                sum_ada(j, 0, 2)
                keep_mod(j - 1, 3)
                sum_ada(j, 2, PIECES)
            ve.wait_ge(sin_ready, 2)
            nc.vector.tensor_scalar(sinT, sinT, rc[:, 1:2], None, ALU.mult).then_inc(rope_ready, 1)
            norm_scale(0)
            rest_unit(0, 0, 0)
            rest_unit(1, 1, 1)
            norm(0, H_N0, 0, SH_M, 0)

            group(U_IN, T_IN, 0, lambda T, b, n: to_z(T, b, n), J_IN, J_IN - 1)
            with ve.Fori(0, 5) as i:
                for g in range(2):
                    group(U_IN + 4 + 4 * g + 8 * i, T_IN + 4 + 4 * g + 8 * i, 4 + 4 * g,
                          lambda T, b, n: to_z(T, b, T), J_IN + 1 + g + 2 * i, J_IN + g + 2 * i)

            def add_rotated(n):
                b = ROPE_ORDER[n]
                ve.wait_ge(cos_done, n + 1)
                ve.wait_ge(rot_used, n + 1)
                zz = z[0:ROPE_DIM, 2 * b:2 * b + 2, :].rearrange("p a t -> p (a t)")
                nc.vector.tensor_tensor(zz, zz, rot[:, n % 2, :], ALU.add).then_inc(rope_done, 1)

            ve.wait_ge(rope_ready, 1)
            for n in range(2 * 6):
                ve.wait_ge(rot_done, n + 1)
                if n >= 2:
                    ve.wait_ge(rope_done, n - 1)
                nc.vector.tensor_tensor(rot[:, n % 2, :].rearrange("p (a t) -> p a t", a=2),
                                        ps[0:ROPE_DIM, 4 + n % 4, :].rearrange("p (a t) -> p a t", a=2),
                                        sinT.unsqueeze(1).to_broadcast([ROPE_DIM, 2, S]), ALU.mult)\
                    .then_inc(rot_used, 1)
                if n:
                    add_rotated(n - 1)
            add_rotated(11)

            for i in range(HEADS + 3):
                if 1 <= i <= HEADS:
                    k = i - 1
                    ve.wait_ge(e_done, 2 * k + 2)
                    nc.vector.reciprocal(rden[:, k, :], den[:, k, :]).then_inc(rden_done, 1)
                    ve.wait_ge(rden_done, k + 1)
                    for q, (a, b) in enumerate(((0, P), (P, 3 * P))):
                        nc.vector.tensor_scalar(prob[:, k % 2, a:b], prob[:, k % 2, a:b], rden[:, k, q:q + 1], None,
                                                ALU.mult).then_inc(p_ready, 1)
                if i >= 3:
                    k = i - 3
                    ve.wait_ge(h_hi, H_MIX + k + 1)
                    nc.vector.tensor_tensor(h[:, k, S:2 * S], ps[:, 4 + k % 2, 0:S], h[:, k, 0:S].bitcast(F32),
                                            ALU.subtract).then_inc(h_ready, 1)
                if i < HEADS:
                    ve.wait_ge(sc_done, i + 1)
                    if i >= 2:
                        ve.wait_ge(pt_done, i - 1)
                    nc.vector.scalar_tensor_tensor(out=prob[:, i % 2, :], in0=ps[:, i % 2, 0:3 * P], scalar=SCALE,
                                                   in1=mask[:, :], op0=ALU.mult, op1=ALU.add).then_inc(sc_used, 1)
                    ve.wait_ge(sc_used, i + 1)
                    for q, (a, b) in enumerate(((0, P), (P, 3 * P))):
                        nc.vector.tensor_reduce(mx[:, i, q:q + 1], prob[:, i % 2, a:b], AX_X, ALU.max).then_inc(mx_done, 1)
                    ve.wait_ge(mx_done, 2 * i + 2)
                    nc.vector.tensor_scalar(nmx[:, i, :], mx[:, i, :], -1.0, None, ALU.mult).then_inc(nmx_ready, 1)
                    if i % 4 == 1:
                        keep_mod(J_ATT - 1 + i // 4, i % 2, 3 * P)
                    sum_ada(J_ATT + i // 4, 2 * (i % 4), 2 * (i % 4) + 2)
            ve.wait_ge(gelu_ready, 1)
            for g in range(GROUPS):
                ve.wait_ge(mixed_done, g + 1)
                nc.vector.tensor_tensor(z[:, 36 + g, :], z[:, 36 + g, :], ps[:, 4 + g, 0:S], ALU.mult).then_inc(gated, 1)
            ve.wait_ge(h_hi, H_MIX + KT)
            nc.vector.tensor_tensor(h[:, HEADS:KT, S:2 * S], z[:, 36:40, :], h[:, HEADS:KT, 0:S].bitcast(F32),
                                    ALU.subtract).then_inc(h_ready, GROUPS)

            with ve.Fori(0, 2) as i:
                for g in range(2):
                    group(U_OUT + 4 * g + 8 * i, T_OUT + 4 * g + 8 * i, 4 + 4 * g,
                          lambda T, b, n: to_x(T, b, X_OUT + 4 * g + n + 8 * i,
                                               mod[:, bass.ds(mod_column(0, G_M, 4 * g + n) + 8 * i, 1)]),
                          J_OUT + g + 2 * i, J_OUT - 1 + g + 2 * i)
            norm(1, H_N1, 0, SH_F, 2)
            with ve.Fori(0, CHUNKS) as c:
                chunk(U_F0 + 12 * c, T_F0 + 24 * c, X_F0 + 16 * c, 0, 4 * c, J_F0 + c, J_F0 - 1 + c)
            norm(2, H_N2, 1, SH_M, 1)
            with ve.Fori(0, 4) as i:
                for g in range(2):
                    group(U_CI + 4 * g + 8 * i, T_CI + 4 * g + 8 * i, 4 + 4 * g,
                          lambda T, b, n: to_z(T, b, 4 * g + n + 8 * i), J_CI + i, J_CI - 1 + i if g == 0 else None,
                          4 * g, 1)

            def taps(N, n0):
                def wt(tap, m):
                    return cwt[:, tap, bass.ds(n0 + m, 1)]

                for m in range(4):
                    ve.wait_ge(conv_prod, N + m + 1)
                    nc.vector.tensor_scalar(gu4[:, m:m + 1, :], z[:, bass.ds(32 + n0 + m, 1), :], wt(2, m), None,
                                            ALU.mult).then_inc(conv_step, 1)
                for d in (1, 2):
                    for m in range(4):
                        ve.wait_ge(conv_step, 2 * N + 4 * (d - 1) + m + 1)
                        nc.vector.scalar_tensor_tensor(
                            out=gu4[:, m:m + 1, d:S], in0=z[:, bass.ds(32 + n0 + m, 1), 0:S - d], scalar=wt(2 - d, m),
                            in1=gu4[:, m:m + 1, d:S], op0=ALU.mult, op1=ALU.add)\
                            .then_inc(conv_step if d == 1 else conv_sum, 1)

            def split_conv(n):
                ve.wait_ge(h_hi, H_CONV + 4 * n + 4)
                nc.vector.tensor_tensor(h[:, 4 * n:4 * n + 4, S:2 * S], z[:, 4 * n:4 * n + 4, :],
                                        h[:, 4 * n:4 * n + 4, 0:S].bitcast(F32), ALU.subtract).then_inc(h_ready, 4)

            for g in range(4):
                group(U_CI2 + 4 * g, T_CI2 + 4 * g, 4 + 4 * g, lambda T, b, n: to_z(T, b, 32 + 4 * g + n),
                      J_CI2 + g // 2, J_CI2 - 1 + g // 2 if g % 2 == 0 else None, 4 * (g % 2), 1)
                if g == 3:
                    for n in range(3):
                        split_conv(n)
                taps(4 * g, 4 * g)
            split_conv(3)
            for g in range(4):
                group(U_CO + 4 * g, T_CO + 4 * g, 4 + 4 * g,
                      lambda T, b, n: to_x(T, b, X_CO + 4 * g + n,
                                           mod[:, mod_column(1, G_M, 4 * g + n):mod_column(1, G_M, 4 * g + n) + 1]),
                      J_CO + g, J_CO - 1 + g)
            keep_mod(J_END - 1, 4)
            norm(3, H_N3, 1, SH_F, 3)
            with ve.Fori(0, CHUNKS - 1) as c:
                chunk(U_F1 + 12 * c, T_F1 + 24 * c, X_F1 + 16 * c, 1, 4 * CHUNKS + 4 * c)
            chunk(U_END - 12, T_END - 24, X_END - 16, 1, 8 * CHUNKS - 4, last=True)
            norm_scale(4)
            ve.wait_ge(rstd_ready, 5)
            for n in range(KT):
                nc.vector.scalar_tensor_tensor(out=z[:, 32 + n, :], in0=x[:, n, :], scalar=gain[:, 4, n:n + 1],
                                               in1=rstd[:, :], op0=ALU.mult, op1=ALU.mult).then_inc(out_ready, 1)

        @block.tensor
        def _(pe):
            def pair(b, s, k, col, rhs, start, stop):
                nc.tensor.matmul(ps[:, b, :], whi[s][:, k, col:col + P], rhs, start=start, stop=False)
                return nc.tensor.matmul(ps[:, b, 0:S], wlo[s][:, k, col:col + P], rhs[:, 0:S], start=False, stop=stop)

            def reduce_ada(j, b, col=0):
                pe.wait_ge(acc_ready, j + 1)
                for n in range(4):
                    last = nc.tensor.matmul(ps[:, b, col + n:col + n + 1], acc[:, 2, n * P:(n + 1) * P], ones[:, 0:1],
                                            start=True, stop=True)
                last.then_inc(red_done, 1)

            def group(u, T, b, ready=None, kept=None, before=None):
                for k in range(4):
                    pe.wait_ge(lo_ready, u + k + 1)
                    if k == 0:
                        if ready is not None:
                            pe.wait_ge(h_ready, ready + 1)
                    if k == 2 and kept is not None:
                        pe.wait_ge(tile_free, BANKS + T)
                        reduce_ada(kept, (b + 7) % BANKS)
                    for n in range(4):
                        if k == 0:
                            pe.wait_ge(tile_free, T + n + 1)
                            if n == 3 and before is not None:
                                pe.wait_ge(mod_done, before + 1)
                        for t in range(4):
                            if n == 0 and ready is not None:
                                pe.wait_ge(h_ready, ready + 4 * k + t + 1)
                            last = pair((b + n) % BANKS, k % PAIR, t, P * n, h[:, 4 * k + t, :],
                                        k == 0 and t == 0, k == 3 and t == 3)
                        if k == 3:
                            last.then_inc(tile_done, 1)
                    if k < 3:
                        last.then_inc(unit_used, 1)

            def chunk(u, T, ready, F, kept=None):
                for g in range(2):
                    b = 4 + 4 * g
                    for k in range(4):
                        pe.wait_ge(lo_ready, u + 4 * g + k + 1)
                        if k == 0 and g == 0:
                            pe.wait_ge(h_ready, ready + 1)
                        if k == 2 and g == 0 and kept is not None:
                            pe.wait_ge(tile_free, BANKS + T)
                            reduce_ada(kept, (b + 7) % BANKS)
                        for n in range(4):
                            if k == 0:
                                pe.wait_ge(tile_free, T + 4 * g + n + 1)
                                if n == 3 and g == 1 and kept is not None:
                                    pe.wait_ge(mod_done, kept + 1)
                            for t in range(4):
                                if n == 0 and g == 0:
                                    pe.wait_ge(h_ready, ready + 4 * k + t + 1)
                                last = pair((b + n) % BANKS, k % PAIR, t, P * (n // 2) + 256 * (n % 2),
                                            h[:, 4 * k + t, :], k == 0 and t == 0, k == 3 and t == 3)
                            if k == 3:
                                last.then_inc(tile_done, 1)
                        if k < 3:
                            last.then_inc(unit_used, 1)
                for g in range(4):
                    b = 4 + 4 * g
                    pe.wait_ge(lo_ready, u + 8 + g + 1)
                    order = [(n, t) for t in range(4) for n in range(4)] if g == 0 else \
                        [(n, t) for n in range(4) for t in range(4)]
                    for n, t in order:
                        if g == 0 and n == 0:
                            pe.wait_ge(act_ready, F + t + 1)
                        if t == 0:
                            pe.wait_ge(tile_free, T + 8 + 4 * g + n + 1)
                        last = pair((b + n) % BANKS, g % PAIR, t, P * n, act[:, t, :], t == 0, t == 3)
                        if t == 3:
                            last.then_inc(tile_done, 1)

            def norm(k, T):
                pe.wait_ge(tile_free, T + 4)
                for n in range(KT):
                    pe.wait_ge(sq_ready, 7 * k + (n // 4 + 1 if n < 12 else n - 8))
                    last = nc.tensor.matmul(ps[:, NORM_BANK, 0:S], ones[:, :], z[:, n, :], start=(n == 0),
                                            stop=(n == KT - 1))
                last.then_inc(ms_ready, 1)

            pe.wait_ge(pool_const, 1)
            pe.wait_ge(tile_free, BANKS)
            with pe.Fori(0, J_IN - 1) as j:
                reduce_ada(j, 3)
            norm(0, T_IN)
            group(U_IN, T_IN, 0, H_N0, J_IN - 1)
            with pe.Fori(0, 5) as i:
                for g in range(2):
                    group(U_IN + 4 + 4 * g + 8 * i, T_IN + 4 + 4 * g + 8 * i, 4 + 4 * g, None, J_IN + g + 2 * i,
                          J_IN - 1 + g + 2 * i)

            pe.wait_ge(const_loaded, 16 * N_CONST)
            pe.wait_ge(tile_free, BANKS + T_OUT)
            for n, b in enumerate(ROPE_ORDER):
                if n >= 4:
                    pe.wait_ge(rot_used, n - 3)
                nc.tensor.matmul(ps[0:ROPE_DIM, 4 + n % 4, :], rc[:, 2:2 + ROPE_DIM],
                                 z[0:ROPE_DIM, 2 * b:2 * b + 2, :].rearrange("p a t -> p (a t)"),
                                 start=True, stop=True).then_inc(rot_done, 1)

            pe.wait_ge(rot_used, 12)
            for i in range(HEADS + 2):
                if i < HEADS:
                    if i >= 2:
                        pe.wait_ge(v_ready, i - 1)
                    for n in range(2):
                        last = nc.tensor.transpose(ps[:, 6 + i % 2, n * P:(n + 1) * P],
                                                   z[:, 24 + i, n * P:(n + 1) * P], ident[:, :])
                    last.then_inc(v_done, 1)
                    if i == 0:
                        pe.wait_ge(rope_done, 12)
                    if i >= 2:
                        pe.wait_ge(sc_used, i - 1)
                    if i % 4 == 3:
                        pe.wait_ge(mod_done, J_ATT + i // 4)
                    if i % 4 == 1:
                        reduce_ada(J_ATT - 1 + i // 4, i % 2, 3 * P)
                    nc.tensor.matmul(ps[:, i % 2, 0:P], z[:, i, 0:P], z[:, 12 + i, 0:P], start=True, stop=True)
                    nc.tensor.matmul(ps[:, i % 2, P:3 * P], z[:, i, P:S], z[:, 12 + i, :], start=True, stop=True)\
                        .then_inc(sc_done, 1)
                if 1 <= i <= HEADS:
                    k = i - 1
                    pe.wait_ge(p_ready, 2 * k + 2)
                    if k >= 2:
                        pe.wait_ge(pt_ready, k - 1)
                    for n in range(3):
                        last = nc.tensor.transpose(ps[:, 2 + k % 2, n * P:(n + 1) * P],
                                                   prob[:, k % 2, n * P:(n + 1) * P], ident[:, :])
                    last.then_inc(pt_done, 1)
                if i >= 2:
                    k = i - 2
                    pe.wait_ge(pt_ready, k + 1)
                    pe.wait_ge(v_ready, k + 1)
                    if k >= 2:
                        pe.wait_ge(h_ready, H_MIX + k - 1)
                    nc.tensor.matmul(ps[:, 4 + k % 2, 0:S], vtok[:, k % 2, 0:P], probT[:, k % 2, 0:S],
                                     start=True, stop=False)
                    nc.tensor.matmul(ps[:, 4 + k % 2, P:S], vtok[:, k % 2, P:S], probT[:, k % 2, S:3 * P],
                                     start=False, stop=True).then_inc(o_done, 1)

            pe.wait_ge(gelu_ready, 1)
            pe.wait_ge(tril_ready, 1)
            pe.wait_ge(sc_used, HEADS)
            pe.wait_ge(pt_ready, HEADS)
            for n in range(3):
                for m in range(4):
                    g, half_t = 2 * n + m // 2, m % 2
                    src = wsr[:, m * P:(m + 1) * P] if n == 2 else z[:, 40 + g, half_t * P:(half_t + 1) * P]
                    last = nc.tensor.transpose(ps[:, n, m * P:(m + 1) * P], src, ident[:, :])
                last.then_inc(sgt_done, 1)
            pe.wait_ge(sgt_ready, 3)
            pe.wait_ge(v_ready, HEADS)
            pe.wait_ge(h_ready, H_MIX + HEADS)
            for g in range(GROUPS):
                for n in range(2):
                    nc.tensor.matmul(ps[:, 4 + g, n * P:(n + 1) * P], vgt[:, g, n * P:(n + 1) * P],
                                     wst[:, g * P:(g + 1) * P], start=True, stop=False)
                    last = nc.tensor.matmul(ps[:, 4 + g, n * P:(n + 1) * P], ones[ROPE_DIM:ROPE_DIM + 1, :],
                                            sgub[:, g * P:(g + 1) * P], start=False, stop=True)
                last.then_inc(mixed_done, 1)
            pe.wait_ge(gated, GROUPS)

            with pe.Fori(0, 2) as i:
                for g in range(2):
                    group(U_OUT + 4 * g + 8 * i, T_OUT + 4 * g + 8 * i, 4 + 4 * g, H_MIX if g == 0 else None,
                          J_OUT - 1 + g + 2 * i, J_OUT - 2 + g + 2 * i)
            pe.wait_ge(mod_done, J_F0 - 1)
            norm(1, T_F0)
            with pe.Fori(0, CHUNKS) as c:
                chunk(U_F0 + 12 * c, T_F0 + 24 * c, H_N1, 4 * c, J_F0 - 1 + c)
            norm(2, T_CI)
            with pe.Fori(0, 4) as i:
                for g in range(2):
                    group(U_CI + 4 * g + 8 * i, T_CI + 4 * g + 8 * i, 4 + 4 * g, *((H_N2, J_CI - 1 + i) if g == 0 else
                                                                                       (None, None, J_CI - 1 + i)))
            with pe.Fori(0, 2) as i:
                for g in range(2):
                    group(U_CI2 + 4 * g + 8 * i, T_CI2 + 4 * g + 8 * i, 4 + 4 * g,
                          *((None, J_CI2 - 1 + i) if g == 0 else (None, None, J_CI2 - 1 + i)))
            for g in range(4):
                group(U_CO + 4 * g, T_CO + 4 * g, 4 + 4 * g, H_CONV if g == 0 else None, J_CO - 1 + g,
                      J_CO - 2 + g if g else None)
            pe.wait_ge(tile_free, BANKS + T_F1 - 4)
            reduce_ada(J_END - 1, 4)
            pe.wait_ge(mod_done, J_END - 1)
            norm(3, T_F1)
            pe.wait_ge(mod_done, J_END)
            with pe.Fori(0, CHUNKS) as c:
                chunk(U_F1 + 12 * c, T_F1 + 24 * c, H_N3, 4 * CHUNKS + 4 * c)
            norm(4, T_END)


def mask_constant():
    dist = np.arange(S)[:, None] - np.arange(S)[None, :]
    count = sum((dist >= 0) & (dist % d == 0) & (dist // d <= w // d) for w, d in BRANCHES)
    m = np.where(count > 0, np.log(np.maximum(count, 1)), MASKED).astype(np.float32)
    return np.concatenate([m[:P, :P], m[P:]], axis=1)


def rope_constants():
    n = ROPE_DIM // 2
    freq = (np.float32(ROPE_THETA) ** (-np.arange(0, ROPE_DIM, 2, dtype=np.float32) / np.float32(ROPE_DIM)))
    swap = np.roll(np.eye(ROPE_DIM, dtype=np.float32), n, axis=1)
    sign = np.repeat(np.array([-1, 1], np.float32), n)
    return np.concatenate([np.tile(freq.astype(np.float32), 2)[:, None], sign[:, None], swap], axis=1)


def kernel(**inputs):
    import concourse.bacc as bacc
    from concourse.bass_utils import run_bass_kernel_spmd

    a = {k: np.asarray(v) for k, v in inputs.items()}

    def columns(v):
        return np.moveaxis(v.reshape(*v.shape[:-1], -1, P), -1, 0)

    arrays = {
        "xT": a["x"][0].T,
        "c_col": columns(a["c"][0]),
        "pos": np.broadcast_to(a["positions"], (ROPE_DIM, S)),
        "ada_w": a["ada_w"],
        "ada_b": columns(a["ada_b"]).reshape(P, -1),
        "g_mix": columns(a["norm_mix"]),
        "g_ffn": columns(a["norm_ffn"]),
        "w_in": a["ab_w_in"][0],
        "sgu_w": np.moveaxis(a["sgu_w"][0], 0, 1),
        "sgu_b": a["sgu_b"][0].reshape(1, -1),
        "w_out": a["ab_w_out"][0],
        "conv_in": a["conv_w_in"][0],
        "conv_w": columns(a["conv_w"][0]),
        "conv_out": a["conv_w_out"][0],
        "ff_gate": a["ffn_w_gate"],
        "ff_up": a["ffn_w_up"],
        "ff_down": a["ffn_w_down"],
        "g_fin": columns(a["final_norm"]),
        "rope_const": rope_constants(),
        "ident_in": np.eye(P, dtype=np.float32),
        "mask_in": mask_constant(),
    }
    arrays = {k: np.ascontiguousarray(v) for k, v in arrays.items()}
    nc = bacc.Bacc("TRN2", target_bir_lowering=False, num_devices=1, dynamic_dma_scratch_size=1024)
    aps = {k: nc.dram_tensor(k, v.shape, mybir.dt.from_np(v.dtype), kind="ExternalInput").ap()
           for k, v in arrays.items()}
    outT = nc.dram_tensor("outT", (D, S), F32, kind="ExternalOutput").ap()
    decoder_kernel(nc, **aps, outT=outT)
    r = run_bass_kernel_spmd(nc, [arrays], core_ids=[0])
    return np.ascontiguousarray(r.results[0]["outT"].T)[None]
```
